# Optimizing a Trainium2 kernel written in Bass

```python
import math
import jax, jax.numpy as jnp
from jax import lax
import numpy as np

D_MODEL = 2048
BATCH = 1
SEQ = 512
DEPTH = 2

CHUNK = 64
Q_BLOCK = 128
N_MIXERS = 4
EPS = 1e-6
ROPE_BASE = 10000.0

SB_HEADS = 16
SB_HEAD_DIM = D_MODEL // SB_HEADS
SB_WIDTH = SB_HEADS * SB_HEAD_DIM
SC_WIDTH = D_MODEL
CONV_WIDTH = 3
MLA_HEADS = 16
MLA_NOPE_DIM = 128
MLA_ROPE_DIM = 64
MLA_V_DIM = 128
MLA_Q_RANK = D_MODEL // 4
MLA_KV_RANK = D_MODEL // 8
MLA_WIDTH = MLA_HEADS * MLA_V_DIM
MLA_IN_WIDTH = MLA_Q_RANK + MLA_KV_RANK + MLA_ROPE_DIM + MLA_WIDTH
RET_HEADS = 8
RET_QK_DIM = D_MODEL // RET_HEADS
RET_V_DIM = 2 * RET_QK_DIM
RET_QK_WIDTH = RET_HEADS * RET_QK_DIM
RET_V_WIDTH = RET_HEADS * RET_V_DIM

kernel_name = 'hybrid_interleaved_streaming_trunk'

def n_layers_of(kind):
    return len(range(kind, DEPTH, N_MIXERS))

def rmsnorm(x, g):
    xf = x.astype(jnp.float32)
    y = xf * lax.rsqrt(jnp.mean(xf * xf, axis=-1, keepdims=True) + EPS)
    return (y * g.astype(jnp.float32)).astype(x.dtype)

def rope(x, positions):
    half = x.shape[-1] // 2
    inv_freq = jnp.exp(-math.log(ROPE_BASE) * jnp.arange(half, dtype=jnp.float32) / half)
    ang = positions.astype(jnp.float32)[:, :, None, None] * inv_freq
    cos, sin = jnp.cos(ang), jnp.sin(ang)
    xf = x.astype(jnp.float32)
    x1, x2 = xf[..., :half], xf[..., half:]
    return jnp.concatenate([x1 * cos - x2 * sin, x1 * sin + x2 * cos], axis=-1).astype(x.dtype)

def stick_breaking_mixer(xn, w_in, w_out):
    b, s, _ = xn.shape
    q, k, v, gate = jnp.split(xn @ w_in, 4, axis=-1)
    q = q.reshape(b, s, SB_HEADS, SB_HEAD_DIM)
    k = k.reshape(b, s, SB_HEADS, SB_HEAD_DIM)
    v = v.reshape(b, s, SB_HEADS, SB_HEAD_DIM)
    scale = 1.0 / math.sqrt(SB_HEAD_DIM)
    outs = []
    for blk in range(s // Q_BLOCK):
        lo, hi = blk * Q_BLOCK, (blk + 1) * Q_BLOCK
        z = jnp.einsum('bqhd,bkhd->bhqk', q[:, lo:hi].astype(jnp.float32),
                       k[:, :hi].astype(jnp.float32)) * scale
        strict = jnp.arange(hi)[None, :] < jnp.arange(lo, hi)[:, None]
        log_beta = jax.nn.log_sigmoid(z)
        log_1m_beta = jnp.where(strict, jax.nn.log_sigmoid(-z), 0.0)
        between = lax.cumsum(log_1m_beta, axis=3, reverse=True) - log_1m_beta
        a = jnp.where(strict, jnp.exp(log_beta + between), 0.0)
        o = jnp.einsum('bhqk,bkhd->bqhd', a, v[:, :hi].astype(jnp.float32))
        outs.append(o.astype(xn.dtype))
    o = jnp.concatenate(outs, axis=1).reshape(b, s, SB_WIDTH)
    return (o * jax.nn.silu(gate)) @ w_out

def short_conv_mixer(xn, w_in, conv_w, conv_b, w_out):
    b_gate, c_gate, u, gate = jnp.split(xn @ w_in, 4, axis=-1)
    cu = c_gate * u
    y = lax.conv_general_dilated(cu, conv_w[:, None, :], window_strides=(1,),
                                 padding=[(CONV_WIDTH - 1, 0)],
                                 dimension_numbers=('NWC', 'WIO', 'NWC'),
                                 feature_group_count=SC_WIDTH) + conv_b
    return (b_gate * y * jax.nn.silu(gate)) @ w_out

def mla_mixer(xn, positions, w_in, q_norm, w_uq, kv_norm, w_ukv,
              qn_nope, qn_rope, kn_nope, kn_rope, w_out):
    b, s, _ = xn.shape
    c_q, c_kv, k_rope, gate = jnp.split(
        xn @ w_in, [MLA_Q_RANK, MLA_Q_RANK + MLA_KV_RANK, MLA_Q_RANK + MLA_KV_RANK + MLA_ROPE_DIM], axis=-1)
    q = (rmsnorm(c_q, q_norm) @ w_uq).reshape(b, s, MLA_HEADS, MLA_NOPE_DIM + MLA_ROPE_DIM)
    kv = (rmsnorm(c_kv, kv_norm) @ w_ukv).reshape(b, s, MLA_HEADS, MLA_NOPE_DIM + MLA_V_DIM)
    q_nope = rmsnorm(q[..., :MLA_NOPE_DIM], qn_nope)
    q_rot = rope(rmsnorm(q[..., MLA_NOPE_DIM:], qn_rope), positions)
    k_nope = rmsnorm(kv[..., :MLA_NOPE_DIM], kn_nope)
    v = kv[..., MLA_NOPE_DIM:]
    k_rot = rope(rmsnorm(k_rope, kn_rope)[:, :, None, :], positions)[:, :, 0]
    scale = 1.0 / math.sqrt(MLA_NOPE_DIM + MLA_ROPE_DIM)
    outs = []
    for blk in range(s // Q_BLOCK):
        lo, hi = blk * Q_BLOCK, (blk + 1) * Q_BLOCK
        sc = (jnp.einsum('bqhd,bkhd->bhqk', q_nope[:, lo:hi].astype(jnp.float32),
                         k_nope[:, :hi].astype(jnp.float32))
              + jnp.einsum('bqhr,bkr->bhqk', q_rot[:, lo:hi].astype(jnp.float32),
                           k_rot[:, :hi].astype(jnp.float32))) * scale
        chunk_ok = (jnp.arange(hi)[None, :] // CHUNK) <= (jnp.arange(lo, hi)[:, None] // CHUNK)
        p = jax.nn.softmax(jnp.where(chunk_ok, sc, -jnp.inf), axis=-1)
        o = jnp.einsum('bhqk,bkhd->bqhd', p, v[:, :hi].astype(jnp.float32))
        outs.append(o.astype(xn.dtype))
    o = jnp.concatenate(outs, axis=1).reshape(b, s, MLA_WIDTH)
    return (o * jax.nn.silu(gate)) @ w_out

def retention_mixer(xn, positions, w_in, out_norm, w_out):
    b, s, _ = xn.shape
    q, k, v, gate = jnp.split(
        xn @ w_in, [RET_QK_WIDTH, 2 * RET_QK_WIDTH, 2 * RET_QK_WIDTH + RET_V_WIDTH], axis=-1)
    q = rope(q.reshape(b, s, RET_HEADS, RET_QK_DIM), positions)
    k = rope(k.reshape(b, s, RET_HEADS, RET_QK_DIM), positions) * (RET_QK_DIM ** -0.5)
    v = v.reshape(b, s, RET_HEADS, RET_V_DIM)
    n_chunks = s // CHUNK

    def to_chunks(t):
        return t.reshape(b, n_chunks, CHUNK, RET_HEADS, t.shape[-1]).transpose(1, 0, 3, 2, 4).astype(jnp.float32)

    log_gamma = jnp.log1p(-jnp.exp2(-5.0 - jnp.arange(RET_HEADS, dtype=jnp.float32)))
    n = jnp.arange(CHUNK, dtype=jnp.float32)
    rel = n[:, None] - n[None, :]
    decay_mask = jnp.where(rel >= 0, jnp.exp(log_gamma[:, None, None] * jnp.maximum(rel, 0.0)), 0.0)
    q_decay = jnp.exp(log_gamma[:, None] * (n + 1.0))[..., None]
    k_decay = jnp.exp(log_gamma[:, None] * (CHUNK - 1.0 - n))[..., None]
    chunk_decay = jnp.exp(log_gamma * CHUNK)[:, None, None]

    def step(state, qkv):
        qc, kc, vc = qkv
        intra = jnp.einsum('bhnd,bhmd->bhnm', qc, kc) * decay_mask
        out = (jnp.einsum('bhnm,bhmv->bhnv', intra, vc)
               + jnp.einsum('bhnd,bhdv->bhnv', qc, state) * q_decay)
        state = state * chunk_decay + jnp.einsum('bhmd,bhmv->bhdv', kc * k_decay, vc)
        return state, out

    state0 = jnp.zeros((b, RET_HEADS, RET_QK_DIM, RET_V_DIM), jnp.float32)
    _, o = lax.scan(step, state0, (to_chunks(q), to_chunks(k), to_chunks(v)))
    o = o.transpose(1, 0, 3, 2, 4).reshape(b, s, RET_HEADS, RET_V_DIM)
    o = rmsnorm(o, out_norm.reshape(RET_HEADS, RET_V_DIM)).astype(xn.dtype).reshape(b, s, RET_V_WIDTH)
    return (jax.nn.silu(gate) * o) @ w_out

def setup_inputs(seed: int = 0) -> dict:
    key = jax.random.key(seed)
    keys = iter(jax.random.split(key, 32))

    def dense(shape, fan_in):
        return jax.random.normal(next(keys), shape, jnp.float32) * (fan_in ** -0.5)

    def gain(shape):
        return 1.0 + 0.02 * jax.random.normal(next(keys), shape, jnp.float32)

    na, nb, nc, nd = (n_layers_of(m) for m in range(N_MIXERS))
    x = jax.random.normal(next(keys), (BATCH, SEQ, D_MODEL), jnp.float32)
    offsets = jax.random.randint(next(keys), (BATCH, 1), 0, 4096, dtype=jnp.int32)
    positions = (offsets + jnp.arange(SEQ, dtype=jnp.int32)[None, :]).astype(jnp.int32)
    return {
        'x': x,
        'positions': positions,
        'norm_g': gain((DEPTH, D_MODEL)),
        'sb_w_in': dense((na, D_MODEL, 4 * SB_WIDTH), D_MODEL),
        'sb_w_out': dense((na, SB_WIDTH, D_MODEL), SB_WIDTH),
        'sc_w_in': dense((nb, D_MODEL, 4 * SC_WIDTH), D_MODEL),
        'sc_conv_w': dense((nb, CONV_WIDTH, SC_WIDTH), CONV_WIDTH),
        'sc_conv_b': 0.02 * jax.random.normal(next(keys), (nb, SC_WIDTH), jnp.float32),
        'sc_w_out': dense((nb, SC_WIDTH, D_MODEL), SC_WIDTH),
        'mla_w_in': dense((nc, D_MODEL, MLA_IN_WIDTH), D_MODEL),
        'mla_q_norm': gain((nc, MLA_Q_RANK)),
        'mla_w_uq': dense((nc, MLA_Q_RANK, MLA_HEADS * (MLA_NOPE_DIM + MLA_ROPE_DIM)), MLA_Q_RANK),
        'mla_kv_norm': gain((nc, MLA_KV_RANK)),
        'mla_w_ukv': dense((nc, MLA_KV_RANK, MLA_HEADS * (MLA_NOPE_DIM + MLA_V_DIM)), MLA_KV_RANK),
        'mla_qn_nope': gain((nc, MLA_NOPE_DIM)),
        'mla_qn_rope': gain((nc, MLA_ROPE_DIM)),
        'mla_kn_nope': gain((nc, MLA_NOPE_DIM)),
        'mla_kn_rope': gain((nc, MLA_ROPE_DIM)),
        'mla_w_out': dense((nc, MLA_WIDTH, D_MODEL), MLA_WIDTH),
        'ret_w_in': dense((nd, D_MODEL, 2 * RET_QK_WIDTH + 2 * RET_V_WIDTH), D_MODEL),
        'ret_out_norm': gain((nd, RET_V_WIDTH)),
        'ret_w_out': dense((nd, RET_V_WIDTH, D_MODEL), RET_V_WIDTH),
    }

def reference(x, positions, norm_g, sb_w_in, sb_w_out, sc_w_in, sc_conv_w, sc_conv_b, sc_w_out,
              mla_w_in, mla_q_norm, mla_w_uq, mla_kv_norm, mla_w_ukv, mla_qn_nope, mla_qn_rope,
              mla_kn_nope, mla_kn_rope, mla_w_out, ret_w_in, ret_out_norm, ret_w_out):
    for i in range(DEPTH):
        kind, j = i % N_MIXERS, i // N_MIXERS
        xn = rmsnorm(x, norm_g[i])
        if kind == 0:
            y = stick_breaking_mixer(xn, sb_w_in[j], sb_w_out[j])
        elif kind == 1:
            y = short_conv_mixer(xn, sc_w_in[j], sc_conv_w[j], sc_conv_b[j], sc_w_out[j])
        elif kind == 2:
            y = mla_mixer(xn, positions, mla_w_in[j], mla_q_norm[j], mla_w_uq[j], mla_kv_norm[j],
                          mla_w_ukv[j], mla_qn_nope[j], mla_qn_rope[j], mla_kn_nope[j],
                          mla_kn_rope[j], mla_w_out[j])
        else:
            y = retention_mixer(xn, positions, ret_w_in[j], ret_out_norm[j], ret_w_out[j])
        x = x + y.astype(x.dtype)
    return x


_drawn_inputs = setup_inputs


def setup_inputs(seed=0):
    import zlib

    import numpy as np

    out = dict(_drawn_inputs(seed))
    spreads = {}
    factors = {'sc_conv_b': 5.824}
    for name, (base, spread) in spreads.items():
        noise = np.random.default_rng([zlib.crc32(name.encode()), seed]).standard_normal(out[name].shape)
        drawn = base * np.exp(spread * noise) if base else spread * noise
        out[name] = __import__('jax').numpy.asarray(drawn.astype(out[name].dtype))
    for name, factor in factors.items():
        out[name] = (out[name] * factor).astype(out[name].dtype)
    return out
```

```python
from contextlib import ExitStack

import numpy as np

import concourse.bass as bass
import concourse.mybir as mybir
from concourse.alu_op_type import AluOpType as ALU

ACT = mybir.ActivationFunctionType
F32 = mybir.dt.float32
F32R = mybir.dt.float32r

P = 128
SEQ = 512
D = 2048
KT = D // P
TB = SEQ // P
STRIP = 512
STRIPS = D // STRIP
EPS = 1e-6
MASKED = -1e30
QSCALE = float(P) ** -0.5

PIECE = 512
PIECES = 16
WSLOTS = 4
RAWSLOTS = 2

IN0 = 0
OUT0 = IN0 + KT * PIECES
IN1 = OUT0 + STRIPS * PIECES
OUT1 = IN1 + KT * PIECES

Z_AT = {3: 0, 2: 512, 0: 896, 1: 1024}
Z_COLS = 1280
AT_PSUM = [0, 512, 1024, 1280]
AT_SBUF = [0, 512, 896, 1152]
AT_FROM = [0, 128, 256, 256]
AT_COLS = 1408

BANK_Q, BANK_K, BANK_V, BANK_G = 0, 1, 0, 1
BANK_Z = 2
BANK_O = 5
BANK_B, BANK_C, BANK_U, BANK_SG = 0, 1, 6, 7
SET_A = [0, 1, 6, 7]
SET_B = [2, 3, 4, 5]
BANK_RS0, BANK_RS1 = 6, 2

G_AT, CW_AT, CB_AT, PARAMS = 0, 32, 80, 96


def wait(engine, semaphore, value):
    if isinstance(value, int) and value <= 0:
        return
    engine.wait_ge(semaphore, value)


def trunk(nc, x, norm_g, sb_w_in, sb_w_out, conv_w, conv_b, sc_w_in, sc_w_out, x1_dram, out):
    x_v = x[0].rearrange("(t p) d -> p t d", p=P)
    x1_v = x1_dram.rearrange("(t p) d -> p t d", p=P)
    out_v = out[0].rearrange("(t p) d -> p t d", p=P)
    w_in = [w[0].rearrange("(k p) n -> p k n", p=P) for w in (sb_w_in, sc_w_in)]
    w_out = [w[0].rearrange("(k p) n -> p k n", p=P) for w in (sb_w_out, sc_w_out)]
    
    with ExitStack() as ctx:
        def sb(name, shape, dt=F32):
            return ctx.enter_context(nc.sbuf_tensor(name, shape, dt))

        def sem(name):
            return ctx.enter_context(nc.semaphore(name))

        xh = sb("x_high", [P, KT, SEQ], F32R)
        xl = sb("x_low", [P, KT, SEQ], F32R)
        yh = sb("y_high", [P, KT, SEQ], F32R)
        yl = sb("y_low", [P, KT, SEQ], F32R)
        raw = sb("w_raw", [P, RAWSLOTS, 2 * PIECE])
        wh = sb("w_high", [P, WSLOTS, PIECE], F32R)
        wl = sb("w_low", [P, WSLOTS, PIECE], F32R)
        stage0 = sb("stage0", [P, 2 * Z_COLS])
        stage1 = sb("stage1", [P, 4 * SEQ])
        qh, ql, kh, kl, vh, vl = (sb(n, [P, SEQ], F32R) for n in ("q_high", "q_low", "k_high", "k_low", "v_high", "v_low"))
        ah = sb("a_high", [P, AT_COLS], F32R)
        al = sb("a_low", [P, AT_COLS], F32R)
        ident = sb("ident", [P, P])
        ones = sb("ones", [P, P])
        mask = sb("mask", [P, 3, P])
        rs_b = sb("rs_b", [P, SEQ])
        rs2_b = sb("rs2_b", [P, SEQ])
        diag = sb("diag", [P, SEQ])
        prm_rows = sb("prm_rows", [PARAMS, P])
        prm = sb("prm", [P, PARAMS])
        ssq = sb("ssq", [P, TB, STRIPS])
        rsn = sb("rsn", [P, 5, TB])
        ps = ctx.enter_context(nc.psum_tensor("ps", [P, 8, 512], F32))

        stage = [stage0[:, 0:TB * STRIP].rearrange("p (t n) -> p t n", t=TB),
                 stage1[:, :].rearrange("p (t n) -> p t n", t=TB)]
        ta = stage0[:, 0:Z_COLS]
        tb_ = stage0[:, Z_COLS:2 * Z_COLS]
        f = stage1[:, 0:SEQ]
        fv = stage1[:, SEQ:2 * SEQ]
        gs = stage1[:, 2 * SEQ:3 * SEQ]
        ge = stage1[:, 3 * SEQ:4 * SEQ]
        cu = stage0[:, 0:SEQ + 2]
        t1 = stage0[:, SEQ + 2:2 * SEQ + 2]
        cv = stage0[:, 2 * SEQ + 2:3 * SEQ + 2]
        bb = stage0[:, 3 * SEQ + 2:4 * SEQ + 2]
        z = ps[:, BANK_Z:BANK_Z + 3, :].rearrange("p b n -> p (b n)")

        landed = [sem(f"landed{i}") for i in range(RAWSLOTS)]
        hi_done, lo_done, piece_used = sem("hi_done"), sem("lo_done"), sem("piece_used")
        params_landed, params_t, params_ready = sem("params_landed"), sem("params_t"), sem("params_ready")
        zeroed, consts = sem("zeroed"), sem("consts")
        x_landed = [sem("x_landed0"), sem("x_landed1")]
        x1_stored = [sem("x1_stored0"), sem("x1_stored1")]
        out_stored, last_stored = sem("out_stored"), sem("last_stored")
        x_t, x_hi, x_lo = sem("x_t"), sem("x_hi"), sem("x_lo")
        squares, rs_steps, rs_root, rs_sum = sem("squares"), sem("rs_steps"), sem("rs_root"), sem("rs_sum")
        proj_read = sem("proj_read")
        qk_hi, qk_lo = sem("qk_hi"), sem("qk_lo")
        v_t, v_hi, v_lo = sem("v_t"), sem("v_hi"), sem("v_lo")
        z_done, z_masked, softplus, logits = sem("z_done"), sem("z_masked"), sem("softplus"), sem("logits")
        a_done, a_t, a_hi, a_lo = sem("a_done"), sem("a_t"), sem("a_hi"), sem("a_lo")
        gate_act, gate_steps, conv_steps = sem("gate_act"), sem("gate_steps"), sem("conv_steps")
        av_done, y_read, y_hi, y_lo = sem("av_done"), sem("y_read"), sem("y_hi"), sem("y_lo")
        x1_ready = sem("x1_ready")
        block = ctx.enter_context(nc.Block())

        RS_STEPS = 10

        @block.sync
        def _(sp):
            def load(n0, part, src):
                wait(sp, lo_done, n0 + 2 * part - 2)
                sp.dma_start(raw[:, part % RAWSLOTS, :].rearrange("p (k n) -> p k n", n=src.shape[-1]), src)\
                  .then_inc(landed[part % RAWSLOTS], 16)

            def in_loads(layer, n0, tile, parts=range(8)):
                for part in parts:
                    col = (part // 2) * D + tile * P
                    load(n0, part, w_in[layer][:, 8 * (part % 2):8 * (part % 2) + 8, bass.ds(col, P)])

            def out_loads(layer, n0, strip):
                for part in range(8):
                    load(n0, part, w_out[layer][:, 2 * part:2 * part + 2, bass.ds(strip * STRIP, STRIP)])

            sp.dma_start(prm_rows[G_AT:CW_AT, :], norm_g.rearrange("l (k p) -> (l k) p", p=P)).then_inc(params_landed, 16)
            in_loads(0, IN0, 0, [0])
            sp.dma_start(prm_rows[CW_AT:CB_AT, :], conv_w[0].rearrange("t (k p) -> (t k) p", p=P)).then_inc(params_landed, 16)
            sp.dma_start(prm_rows[CB_AT:PARAMS, :], conv_b[0].rearrange("(k p) -> k p", p=P)).then_inc(params_landed, 16)
            in_loads(0, IN0, 0, range(1, 8))
            with sp.Fori(1, KT) as h:
                in_loads(0, IN0 + PIECES * h, h)
            with sp.Fori(0, STRIPS) as s:
                out_loads(0, OUT0 + PIECES * s, s)
            with sp.Fori(0, KT) as t:
                in_loads(1, IN1 + PIECES * t, t)
            with sp.Fori(0, STRIPS) as s:
                out_loads(1, OUT1 + PIECES * s, s)
            for t in range(TB):
                sp.wait_ge(x1_ready, 2 * TB * STRIPS - TB + t + 1)
                sp.dma_start(out_v[:, t, D - STRIP:D], stage[1][:, t, :]).then_inc(last_stored, 16)
            sp.wait_ge(last_stored, 16 * TB)
            sp.wait_ge(out_stored, 16 * (STRIPS - 1))

        @block.gpsimd
        def _(pool):
            def load_strip(src, s):
                pool.dma_start(stage[s % 2], src[:, :, s * STRIP:(s + 1) * STRIP]).then_inc(x_landed[s % 2], 16)

            load_strip(x_v, 0)
            load_strip(x_v, 1)
            pool.memset(ident[:, :], 0.0).then_inc(zeroed, 1)
            pool.memset(mask[:, :, :], 0.0).then_inc(zeroed, 1)
            pool.memset(ones[:, :], 1.0).then_inc(consts, 1)
            pool.wait_ge(zeroed, 2)
            pool.affine_select(out=ident[:, :], in_=ident[:, :], compare_op=ALU.not_equal, fill=1.0, base=0,
                               pattern=[[-1, P]], channel_multiplier=1).then_inc(consts, 1)
            pool.affine_select(out=mask[:, :, :], in_=mask[:, :, :], compare_op=ALU.is_ge, fill=MASKED, base=-1,
                               pattern=[[0, 3], [-1, P]], channel_multiplier=1).then_inc(consts, 1)
            pool.memset(ah[:, AT_SBUF[3]:AT_SBUF[3] + P].bitcast(F32), 0.0).then_inc(consts, 1)
            pool.memset(al[:, AT_SBUF[3]:AT_SBUF[3] + P].bitcast(F32), 0.0).then_inc(consts, 1)

            for s in (2, 3):
                pool.wait_ge(x_t, 4 * (s - 1))
                pool.wait_ge(squares, TB * (s - 1))
                load_strip(x_v, s)
            pool.wait_ge(a_t, KT)
            load_strip(x_v, 0)
            pool.wait_ge(y_lo, KT)
            load_strip(x_v, 1)
            for s in range(STRIPS):
                pool.wait_ge(x1_ready, TB * (s + 1))
                pool.dma_start(x1_v[:, :, s * STRIP:(s + 1) * STRIP], stage[s % 2]).then_inc(x1_stored[s % 2], 16)
                if s + 2 < STRIPS:
                    pool.wait_ge(x1_stored[s % 2], 16 * (s // 2 + 1))
                    pool.wait_ge(x_t, KT + 4 * (s + 1))
                    pool.wait_ge(squares, TB * (STRIPS + s + 1))
                    load_strip(x_v, s + 2)
            for i in range(2):
                pool.wait_ge(x1_stored[i], 32)
            pool.wait_ge(y_lo, 2 * KT)
            load_strip(x1_v, 0)
            load_strip(x1_v, 1)
            for s in range(STRIPS - 1):
                pool.wait_ge(x1_ready, TB * (STRIPS + s + 1))
                pool.dma_start(out_v[:, :, s * STRIP:(s + 1) * STRIP], stage[s % 2]).then_inc(out_stored, 16)
                if s + 2 < STRIPS:
                    pool.wait_ge(out_stored, 16 * (s + 1))
                    load_strip(x1_v, s + 2)

        @block.scalar
        def _(act):
            def hi(n0, slot):
                load = slot // 2
                if slot % 2 == 0:
                    act.wait_ge(landed[load % RAWSLOTS], landed_value(n0, load))
                wait(act, piece_used, n0 + slot - WSLOTS + 1)
                nc.scalar.copy(wh[:, slot % WSLOTS, :], raw[:, load % RAWSLOTS, PIECE * (slot % 2):PIECE * (slot % 2 + 1)]).then_inc(hi_done, 1)

            def landed_value(n0, load):
                return n0 * 4 + 16 * (load // 2 + 1)

            def softplus_tail(j):
                act.wait_ge(z_masked, j + 1)
                nc.scalar.activation(ta, z[:, 0:Z_COLS], ACT.Abs).then_inc(softplus, 1)
                act.wait_ge(softplus, 3 * j + 1)
                nc.scalar.activation(ta, ta, ACT.Exp, scale=-1.0).then_inc(softplus, 1)
                act.wait_ge(softplus, 3 * j + 2)
                nc.scalar.activation(ta, ta, ACT.Ln, bias=1.0).then_inc(softplus, 1)

            def weights(j):
                act.wait_ge(logits, 3 * j + 3)
                nc.scalar.activation(ta, tb_, ACT.Exp).then_inc(a_done, 1)

            def gate_exp(j):
                act.wait_ge(proj_read, 4 * j + 4)
                nc.scalar.activation(ge, gs, ACT.Exp, scale=-1.0).then_inc(gate_act, 1)

            def v_high(j):
                act.wait_ge(v_t, j + 1)
                nc.scalar.copy(vh[:, :], ps[:, BANK_O, :]).then_inc(v_hi, 1)

            def q_high(h):
                act.wait_ge(proj_read, 4 * h + 1)
                nc.scalar.copy(qh[:, :], f).then_inc(qk_hi, 1)

            def k_high(h):
                act.wait_ge(proj_read, 4 * h + 2)
                nc.scalar.copy(kh[:, :], f).then_inc(qk_hi, 1)

            def a_high(j):
                act.wait_ge(a_t, j + 1)
                nc.scalar.copy(ah[:, 0:896], z[:, 0:896])
                nc.scalar.copy(ah[:, 896:1152], z[:, 1024:1280])
                nc.scalar.copy(ah[:, 1280:1408], z[:, 1280:1408]).then_inc(a_hi, 1)

            def y_high(j, i):
                act.wait_ge(y_read, i + 1)
                nc.scalar.copy(yh[:, bass.ds(j, 1), :].rearrange("p a n -> p (a n)"), f).then_inc(y_hi, 1)

            def x_high(layer, kt):
                act.wait_ge(x_t, KT * layer + kt + 1)
                g = prm[:, G_AT + KT * layer + kt:G_AT + KT * layer + kt + 1]
                nc.scalar.activation(xh[:, kt, :], ps[:, t_bank(layer, kt), :], ACT.Copy, scale=g).then_inc(x_hi, 1)

            def square(layer, s):
                if layer == 0:
                    act.wait_ge(x_landed[s % 2], 16 * (s // 2 + 1))
                for t in range(TB):
                    if layer == 1:
                        act.wait_ge(x1_ready, TB * s + t + 1)
                    wait(act, squares, TB * (layer * STRIPS + s) + t)
                    nc.scalar.activation(diag[:, :], stage[s % 2][:, t, :], ACT.Square,
                                         accum_out=ssq[:, t, s:s + 1]).then_inc(squares, 1)

            def root(layer):
                act.wait_ge(rs_steps, RS_STEPS * layer + 2)
                nc.scalar.activation(rsn[:, 1, :], rsn[:, 0, :], ACT.Sqrt).then_inc(rs_root, 1)

            for s in range(STRIPS):
                for kt in range(4 * s, 4 * s + 4):
                    if s == 0 and kt == 0:
                        act.wait_ge(params_ready, 1)
                    x_high(0, kt)
                hi(IN0, s)
                square(0, s)
            root(0)
            for slot in range(4, PIECES):
                hi(IN0, slot)
                if slot == 7:
                    q_high(0)
                if slot == 11:
                    k_high(0)

            def attend(slot, j, i):
                if slot == 0:
                    softplus_tail(j)
                if slot == 4:
                    gate_exp(j)
                if slot == 5:
                    weights(j)
                if slot == 6:
                    v_high(j)
                if slot == 8:
                    a_high(j)
                if slot == 12:
                    y_high(j, i)

            with act.Fori(1, KT) as h:
                for slot in range(PIECES):
                    hi(IN0 + PIECES * h, slot)
                    if slot == 7:
                        q_high(h)
                    if slot == 11:
                        k_high(h)
                    attend(slot, h - 1, h - 1)

            for s in range(STRIPS):
                for slot in range(PIECES):
                    hi(OUT0 + PIECES * s, slot)
                    if s == 0:
                        attend(slot, KT - 1, KT - 1)
                        continue
                    if slot == 6:
                        square(1, s - 1)
                    if slot == 11:
                        for kt in range(4 * s - 4, 4 * s):
                            x_high(1, kt)

            def gate_silu(t):
                act.wait_ge(proj_read, 4 * (KT + t) + 4)
                nc.scalar.activation(ge, gs, ACT.Silu).then_inc(gate_act, 1)

            for slot in range(PIECES):
                hi(IN1, slot)
                if slot == 4:
                    for kt in range(KT - 4, KT):
                        x_high(1, kt)
                    square(1, STRIPS - 1)
                if slot == 5:
                    root(1)
            with act.Fori(1, KT) as t:
                for slot in range(PIECES):
                    hi(IN1 + PIECES * t, slot)
                    if slot == 3:
                        gate_silu(t - 1)
                    if slot == 4:
                        y_high(t - 1, KT + t - 1)
            for slot in range(PIECES):
                hi(OUT1, slot)
                if slot == 3:
                    gate_silu(KT - 1)
                if slot == 4:
                    y_high(KT - 1, 2 * KT - 1)
            with act.Fori(1, STRIPS) as s:
                for slot in range(PIECES):
                    hi(OUT1 + PIECES * s, slot)

        @block.vector
        def _(dve):
            def lo(n0, slot):
                dve.wait_ge(hi_done, n0 + slot + 1)
                nc.vector.tensor_tensor(wl[:, slot % WSLOTS, :], raw[:, (slot // 2) % RAWSLOTS, PIECE * (slot % 2):PIECE * (slot % 2 + 1)],
                                        wh[:, slot % WSLOTS, :].bitcast(F32), ALU.subtract).then_inc(lo_done, 1)

            def x_low(layer, kt):
                dve.wait_ge(x_hi, KT * layer + kt + 1)
                g = prm[:, G_AT + KT * layer + kt:G_AT + KT * layer + kt + 1]
                nc.vector.scalar_tensor_tensor(xl[:, kt, :], ps[:, t_bank(layer, kt), :], g, xh[:, kt, :].bitcast(F32),
                                               ALU.mult, ALU.subtract).then_inc(x_lo, 1)

            def inverse_rms(layer):
                n = RS_STEPS * layer
                tot, root, inv, tmp, fac = (rsn[:, i, :] for i in range(5))
                dve.wait_ge(squares, TB * STRIPS * (layer + 1))
                nc.vector.reduce_sum(tot, ssq[:, :, :], axis=mybir.AxisListType.X).then_inc(rs_steps, 1)
                dve.wait_ge(rs_steps, n + 1)
                nc.vector.tensor_scalar(tot, tot, 1.0 / D, EPS, ALU.mult, ALU.add).then_inc(rs_steps, 1)
                dve.wait_ge(rs_root, layer + 1)
                nc.vector.reciprocal(inv, root).then_inc(rs_steps, 1)
                dve.wait_ge(rs_steps, n + 3)
                nc.vector.tensor_tensor(tmp, inv, inv, ALU.mult).then_inc(rs_steps, 1)
                dve.wait_ge(rs_steps, n + 4)
                nc.vector.tensor_tensor(fac, tmp, tot, ALU.mult).then_inc(rs_steps, 1)
                dve.wait_ge(rs_steps, n + 5)
                nc.vector.tensor_scalar(fac, fac, -0.5, 1.5, ALU.mult, ALU.add).then_inc(rs_steps, 1)
                dve.wait_ge(rs_steps, n + 6)
                nc.vector.tensor_tensor(inv, inv, fac, ALU.mult).then_inc(rs_steps, 1)
                dve.wait_ge(rs_steps, n + 7)
                for t in range(TB):
                    last = nc.vector.tensor_scalar(diag[:, t * P:(t + 1) * P], ident[:, :], inv[:, t:t + 1], None, ALU.mult)
                last.then_inc(rs_steps, 1)

            def spread_rms(layer):
                n = RS_STEPS * layer
                dve.wait_ge(rs_sum, layer + 1)
                nc.vector.tensor_copy(rs_b[:, :], ps[:, (BANK_RS0, BANK_RS1)[layer], :]).then_inc(rs_steps, 1)
                dve.wait_ge(rs_steps, n + 9)
                nc.vector.tensor_tensor(rs2_b[:, :], rs_b[:, :], rs_b[:, :], ALU.mult).then_inc(rs_steps, 1)
                dve.wait_ge(rs_steps, n + 10)

            def q_read(h):
                dve.wait_ge(piece_used, PIECES * h + 4)
                wait(dve, y_lo, h - 1)
                nc.vector.scalar_tensor_tensor(f, ps[:, BANK_Q, :], QSCALE, rs_b[:, :], ALU.mult, ALU.mult).then_inc(proj_read, 1)

            def q_low(h):
                dve.wait_ge(qk_hi, 2 * h + 1)
                nc.vector.tensor_tensor(ql[:, :], f, qh[:, :].bitcast(F32), ALU.subtract).then_inc(qk_lo, 1)

            def k_read(h):
                dve.wait_ge(piece_used, PIECES * h + 8)
                dve.wait_ge(qk_lo, 2 * h + 1)
                nc.vector.tensor_tensor(f, ps[:, BANK_K, :], rs_b[:, :], ALU.mult).then_inc(proj_read, 1)

            def k_low(h):
                dve.wait_ge(qk_hi, 2 * h + 2)
                nc.vector.tensor_tensor(kl[:, :], f, kh[:, :].bitcast(F32), ALU.subtract).then_inc(qk_lo, 1)

            def v_read(h):
                dve.wait_ge(piece_used, PIECES * h + 12)
                nc.vector.tensor_tensor(fv, ps[:, BANK_V, :], rs_b[:, :], ALU.mult).then_inc(proj_read, 1)

            def g_read(j):
                dve.wait_ge(piece_used, PIECES * j + 16)
                wait(dve, y_read, j)
                nc.vector.tensor_tensor(gs, ps[:, BANK_G, :], rs_b[:, :], ALU.mult).then_inc(proj_read, 1)

            def mask_z(h):
                dve.wait_ge(z_done, h + 1)
                d3 = z[:, 384:1536].rearrange("p (a n) -> p a n", n=384)[:, :, 0:P]
                nc.vector.tensor_tensor(d3, d3, mask[:, :, :], ALU.add)
                d0 = z[:, Z_AT[0]:Z_AT[0] + P]
                nc.vector.tensor_tensor(d0, d0, mask[:, 0, :], ALU.add).then_inc(z_masked, 1)

            def softplus_sum(j):
                dve.wait_ge(softplus, 3 * j + 3)
                nc.vector.scalar_tensor_tensor(tb_, z[:, 0:Z_COLS], 0.0, ta, ALU.max, ALU.add).then_inc(logits, 1)

            def cumulate(j, blocks):
                if 3 in blocks:
                    dve.wait_ge(logits, 3 * j + 1)
                for i in blocks:
                    c0, n = Z_AT[i], P * (i + 1)
                    term = tb_[:, c0:c0 + n][:, ::-1]
                    last = nc.vector.tensor_tensor_scan(ta[:, c0:c0 + n][:, ::-1], term, term, 0.0, ALU.add, ALU.max)
                if 1 in blocks:
                    last.then_inc(logits, 1)

            def subtract(j):
                dve.wait_ge(logits, 3 * j + 2)
                nc.vector.tensor_tensor(tb_, z[:, 0:Z_COLS], ta, ALU.subtract).then_inc(logits, 1)

            def silu(j):
                dve.wait_ge(gate_act, j + 1)
                nc.vector.tensor_scalar(ge, ge, 1.0, None, ALU.add).then_inc(gate_steps, 1)
                dve.wait_ge(gate_steps, 3 * j + 1)
                nc.vector.reciprocal(ge, ge).then_inc(gate_steps, 1)
                dve.wait_ge(gate_steps, 3 * j + 2)
                nc.vector.tensor_tensor(gs, gs, ge, ALU.mult).then_inc(gate_steps, 1)

            def v_low(j):
                dve.wait_ge(v_hi, j + 1)
                nc.vector.tensor_tensor(vl[:, :], ps[:, BANK_O, :], vh[:, :].bitcast(F32), ALU.subtract).then_inc(v_lo, 1)

            def a_low(j):
                dve.wait_ge(a_hi, j + 1)
                nc.vector.tensor_tensor(al[:, 0:896], z[:, 0:896], ah[:, 0:896].bitcast(F32), ALU.subtract)
                nc.vector.tensor_tensor(al[:, 896:1152], z[:, 1024:1280], ah[:, 896:1152].bitcast(F32), ALU.subtract)
                nc.vector.tensor_tensor(al[:, 1280:1408], z[:, 1280:1408], ah[:, 1280:1408].bitcast(F32),
                                        ALU.subtract).then_inc(a_lo, 1)

            def o_read(j):
                dve.wait_ge(av_done, j + 1)
                dve.wait_ge(gate_steps, 3 * j + 3)
                dve.wait_ge(qk_lo, 2 * KT if isinstance(j, int) and j == KT - 1 else 2 * j + 4)
                nc.vector.tensor_tensor(f, ps[:, BANK_O, :], gs, ALU.mult).then_inc(y_read, 1)

            def y_low(j, i):
                dve.wait_ge(y_hi, i + 1)
                nc.vector.tensor_tensor(yl[:, bass.ds(j, 1), :].rearrange("p a n -> p (a n)"), f,
                                        yh[:, bass.ds(j, 1), :].rearrange("p a n -> p (a n)").bitcast(F32),
                                        ALU.subtract).then_inc(y_lo, 1)

            def attend(slot, j, i):
                if slot == 1:
                    softplus_sum(j)
                if slot == 2:
                    cumulate(j, (3,))
                if slot == 3:
                    g_read(j)
                    cumulate(j, (2, 0, 1))
                if slot == 4:
                    subtract(j)
                if slot == 5:
                    silu(j)
                if slot == 6:
                    v_low(j)
                if slot == 9:
                    a_low(j)
                if slot == 12:
                    o_read(j)
                if slot == 13:
                    y_low(j, i)

            def project(slot, h):
                if slot == 7:
                    q_read(h)
                if slot == 8:
                    q_low(h)
                if slot == 11:
                    k_read(h)
                if slot == 12:
                    k_low(h)
                if slot == 15:
                    v_read(h)
                    mask_z(h)

            dve.wait_ge(params_t, 1)
            nc.vector.tensor_copy(prm[:, :], ps[:, 0, 0:PARAMS]).then_inc(params_ready, 1)
            dve.wait_ge(params_ready, 1)
            for s in range(STRIPS):
                for kt in range(4 * s, 4 * s + 4):
                    x_low(0, kt)
                lo(IN0, s)
            inverse_rms(0)
            dve.wait_ge(consts, 5)
            for slot in range(4, PIECES):
                lo(IN0, slot)
                if slot == 7:
                    spread_rms(0)
                project(slot, 0)
            with dve.Fori(1, KT) as h:
                for slot in range(PIECES):
                    lo(IN0 + PIECES * h, slot)
                    project(slot, h)
                    attend(slot, h - 1, h - 1)

            def residual(layer, s):
                banks = out_banks(layer, s)
                dve.wait_ge(piece_used, (OUT0, OUT1)[layer] + PIECES * (s + 1))
                dve.wait_ge(x_landed[s % 2], 16 * (2 * (layer + 1) + s // 2 + 1))
                for t in range(TB):
                    nc.vector.tensor_tensor(stage[s % 2][:, t, :], ps[:, banks[t], :], stage[s % 2][:, t, :],
                                            ALU.add).then_inc(x1_ready, 1)

            for s in range(STRIPS):
                for slot in range(PIECES):
                    lo(OUT0 + PIECES * s, slot)
                    if s == 0:
                        attend(slot, KT - 1, KT - 1)
                        continue
                    if slot == 3:
                        residual(0, s - 1)
                    if slot == 11:
                        for kt in range(4 * s - 4, 4 * s):
                            x_low(1, kt)

            def b_read(t):
                dve.wait_ge(piece_used, IN1 + PIECES * t + 4)
                dve.wait_ge(conv_steps, 4 * t + 1)
                nc.vector.tensor_tensor(bb, ps[:, BANK_B, :], rs_b[:, :], ALU.mult).then_inc(proj_read, 1)

            def c_read(t):
                dve.wait_ge(piece_used, IN1 + PIECES * t + 8)
                nc.vector.tensor_tensor(t1, ps[:, BANK_C, :], rs2_b[:, :], ALU.mult).then_inc(proj_read, 1)

            def u_read(t):
                dve.wait_ge(piece_used, IN1 + PIECES * t + 12)
                dve.wait_ge(proj_read, 4 * (KT + t) + 2)
                nc.vector.tensor_tensor(cu[:, 2:], ps[:, BANK_U, :], t1, ALU.mult).then_inc(proj_read, 1)

            def conv(t):
                def tap(i):
                    return prm[:, bass.ds(CW_AT + KT * i + t, 1)]
                dve.wait_ge(proj_read, 4 * (KT + t) + 3)
                dve.wait_ge(y_read, KT + t)
                nc.vector.tensor_scalar(cv, cu[:, 2:], tap(2), prm[:, bass.ds(CB_AT + t, 1)], ALU.mult, ALU.add).then_inc(conv_steps, 1)
                dve.wait_ge(conv_steps, 4 * t + 2)
                nc.vector.scalar_tensor_tensor(cv, cu[:, 1:SEQ + 1], tap(1), cv, ALU.mult, ALU.add).then_inc(conv_steps, 1)
                dve.wait_ge(conv_steps, 4 * t + 3)
                nc.vector.scalar_tensor_tensor(cv, cu[:, 0:SEQ], tap(0), cv, ALU.mult, ALU.add).then_inc(conv_steps, 1)
                dve.wait_ge(conv_steps, 4 * t + 4)
                nc.vector.tensor_tensor(cv, cv, bb, ALU.mult).then_inc(conv_steps, 1)

            def gate_read(t):
                dve.wait_ge(piece_used, IN1 + PIECES * t + 16)
                nc.vector.tensor_tensor(gs, ps[:, BANK_SG, :], rs_b[:, :], ALU.mult).then_inc(proj_read, 1)

            def mix(t):
                dve.wait_ge(gate_act, KT + t + 1)
                dve.wait_ge(conv_steps, 4 * t + 5)
                dve.wait_ge(y_lo, KT + t)
                nc.vector.tensor_tensor(f, cv, ge, ALU.mult).then_inc(y_read, 1)

            def branch(slot, t):
                if slot == 7:
                    b_read(t)
                if slot == 11:
                    c_read(t)
                if slot == 15:
                    u_read(t)

            def branch_end(slot, t):
                if slot == 0:
                    conv(t)
                if slot == 3:
                    gate_read(t)
                if slot == 4:
                    mix(t)
                if slot == 5:
                    y_low(t, KT + t)

            for slot in range(PIECES):
                lo(IN1, slot)
                if slot == 2:
                    residual(0, STRIPS - 1)
                if slot == 4:
                    for kt in range(KT - 4, KT):
                        x_low(1, kt)
                if slot == 5:
                    inverse_rms(1)
                if slot == 7:
                    spread_rms(1)
                    dve.wait_ge(x1_stored[0], 32)
                    dve.wait_ge(x1_stored[1], 32)
                    nc.vector.memset(cu[:, 0:2], 0.0).then_inc(conv_steps, 1)
                    dve.wait_ge(conv_steps, 1)
                branch(slot, 0)
            with dve.Fori(1, KT) as t:
                for slot in range(PIECES):
                    lo(IN1 + PIECES * t, slot)
                    branch_end(slot, t - 1)
                    branch(slot, t)
            for s in range(STRIPS):
                for slot in range(PIECES):
                    lo(OUT1 + PIECES * s, slot)
                    if s == 0:
                        branch_end(slot, KT - 1)
                    elif slot == 3:
                        residual(1, s - 1)
            residual(1, STRIPS - 1)

        @block.tensor
        def _(pe):
            def three(acc, sh, sl, mh, ml, start, stop):
                nc.tensor.matmul(acc, sh, mh, start=start, stop=False)
                nc.tensor.matmul(acc, sh, ml, start=False, stop=False)
                return nc.tensor.matmul(acc, sl, mh, start=False, stop=stop)

            def in_piece(n0, slot, bank, layer=None):
                pe.wait_ge(lo_done, n0 + slot + 1)
                for i in range(4):
                    kt = 4 * (slot % 4) + i
                    w = slice(i * P, (i + 1) * P)
                    if layer is not None:
                        pe.wait_ge(x_lo, KT * layer + kt + 1)
                    last = three(ps[:, bank, :], wh[:, slot % WSLOTS, w], wl[:, slot % WSLOTS, w],
                                 xh[:, kt, :], xl[:, kt, :], kt == 0, kt == KT - 1)
                last.then_inc(piece_used, 1)

            def out_piece(n0, slot, banks):
                pe.wait_ge(lo_done, n0 + slot + 1)
                for t in range(TB):
                    y = slice(t * P, (t + 1) * P)
                    last = three(ps[:, banks[t], :], yh[:, slot, y], yl[:, slot, y],
                                 wh[:, slot % WSLOTS, :], wl[:, slot % WSLOTS, :], slot == 0, slot == KT - 1)
                last.then_inc(piece_used, 1)

            def transpose_strip(layer, s):
                for kt in range(4 * s, 4 * s + 4):
                    if layer == 0:
                        wait(pe, x_lo, kt - 6)
                    for t in range(TB):
                        last = nc.tensor.transpose(ps[:, t_bank(layer, kt), t * P:(t + 1) * P],
                                                   stage[s % 2][:, t, (kt % 4) * P:(kt % 4 + 1) * P], ident[:, :])
                    last.then_inc(x_t, 1)

            def spread(layer):
                pe.wait_ge(rs_steps, RS_STEPS * layer + 8)
                nc.tensor.matmul(ps[:, (BANK_RS0, BANK_RS1)[layer], :], ones[:, :], diag[:, :], start=True, stop=True).then_inc(rs_sum, 1)

            def logits_of(h):
                pe.wait_ge(qk_lo, 2 * h + 2)
                for i in (3, 2, 0, 1):
                    q, n = slice(i * P, (i + 1) * P), P * (i + 1)
                    last = three(z[:, Z_AT[i]:Z_AT[i] + n], qh[:, q], ql[:, q], kh[:, 0:n], kl[:, 0:n], True, True)
                last.then_inc(z_done, 1)

            def v_transpose(h):
                pe.wait_ge(proj_read, 4 * h + 3)
                wait(pe, y_read, h)
                for t in range(TB):
                    last = nc.tensor.transpose(ps[:, BANK_O, t * P:(t + 1) * P], fv[:, t * P:(t + 1) * P], ident[:, :])
                last.then_inc(v_t, 1)

            def a_transpose(j):
                pe.wait_ge(a_done, j + 1)
                for kb in range(TB):
                    for i in range(kb, TB):
                        last = nc.tensor.transpose(z[:, AT_PSUM[kb] + P * (i - kb):AT_PSUM[kb] + P * (i - kb + 1)],
                                                   ta[:, Z_AT[i] + P * kb:Z_AT[i] + P * (kb + 1)], ident[:, :])
                last.then_inc(a_t, 1)

            def output_of(j):
                pe.wait_ge(v_lo, j + 1)
                pe.wait_ge(a_lo, j + 1)
                for kb in range(TB):
                    q0, c0, v = AT_FROM[kb], AT_SBUF[kb], slice(kb * P, (kb + 1) * P)
                    n = SEQ - q0
                    last = three(ps[:, BANK_O, q0:SEQ], vh[:, v], vl[:, v], ah[:, c0:c0 + n], al[:, c0:c0 + n], kb == 0, kb == TB - 1)
                last.then_inc(av_done, 1)

            pe.wait_ge(consts, 5)
            pe.wait_ge(params_landed, 48)
            nc.tensor.transpose(ps[:, 0, 0:PARAMS], prm_rows[:, :], ident[0:PARAMS, 0:PARAMS]).then_inc(params_t, 1)
            pe.wait_ge(x_landed[0], 16)
            transpose_strip(0, 0)
            pe.wait_ge(x_landed[1], 16)
            transpose_strip(0, 1)
            pe.wait_ge(params_ready, 1)
            in_piece(IN0, 0, BANK_Q, layer=0)
            pe.wait_ge(x_landed[0], 32)
            transpose_strip(0, 2)
            in_piece(IN0, 1, BANK_Q, layer=0)
            pe.wait_ge(x_landed[1], 32)
            transpose_strip(0, 3)
            in_piece(IN0, 2, BANK_Q, layer=0)
            in_piece(IN0, 3, BANK_Q, layer=0)
            for slot in range(4, PIECES):
                if slot == 8:
                    pe.wait_ge(proj_read, 1)
                if slot == 12:
                    pe.wait_ge(proj_read, 2)
                    logits_of(0)
                in_piece(IN0, slot, (BANK_Q, BANK_K, BANK_V, BANK_G)[slot // 4])
                if slot == 5:
                    spread(0)
            v_transpose(0)
            with pe.Fori(1, KT) as h:
                for slot in range(PIECES):
                    if slot == 4:
                        a_transpose(h - 1)
                    if slot == 8:
                        output_of(h - 1)
                    if slot == 12:
                        logits_of(h)
                    if slot % 4 == 0:
                        pe.wait_ge(proj_read, 4 * h - 1 + slot // 4)
                    in_piece(IN0 + PIECES * h, slot, (BANK_Q, BANK_K, BANK_V, BANK_G)[slot // 4])
                v_transpose(h)
            pe.wait_ge(proj_read, 4 * KT)
            for slot in range(PIECES):
                if slot == 4:
                    a_transpose(KT - 1)
                if slot == 8:
                    output_of(KT - 1)
                if slot == 0:
                    pe.wait_ge(y_lo, KT - 1)
                if slot == 15:
                    pe.wait_ge(y_lo, KT)
                out_piece(OUT0, slot, out_banks(0, 0))
            for s in range(1, STRIPS):
                if s > 1:
                    pe.wait_ge(x_lo, KT + 4 * (s - 1))
                else:
                    pe.wait_ge(y_read, KT)
                for slot in range(PIECES):
                    if slot == 8:
                        pe.wait_ge(x1_ready, TB * s)
                        transpose_strip(1, s - 1)
                    out_piece(OUT0 + PIECES * s, slot, out_banks(0, s))

            CONV_BANKS = (BANK_B, BANK_C, BANK_U, BANK_SG)
            pe.wait_ge(x_lo, KT + 4 * (STRIPS - 1))
            for slot in range(PIECES):
                if slot == 2:
                    pe.wait_ge(x1_ready, TB * STRIPS)
                    transpose_strip(1, STRIPS - 1)
                in_piece(IN1, slot, CONV_BANKS[slot // 4], layer=1 if slot < 4 else None)
                if slot == 6:
                    spread(1)
            with pe.Fori(1, KT) as t:
                for slot in range(PIECES):
                    if slot % 4 == 0:
                        pe.wait_ge(proj_read, 4 * (KT + t) - 3 + slot // 4)
                    in_piece(IN1 + PIECES * t, slot, CONV_BANKS[slot // 4])
            for s in range(STRIPS):
                if s == 0:
                    pe.wait_ge(y_lo, 2 * KT - 1)
                if s == 1:
                    pe.wait_ge(proj_read, 8 * KT)
                if s > 1:
                    pe.wait_ge(x1_ready, TB * (STRIPS + s - 1))
                for slot in range(PIECES):
                    if s == 0 and slot == 15:
                        pe.wait_ge(y_lo, 2 * KT)
                    out_piece(OUT1 + PIECES * s, slot, out_banks(1, s))


def t_bank(layer, kt):
    if layer == 0:
        return 1 + kt % 7
    return out_banks(0, kt // 4)[kt % 4]


def out_banks(layer, s):
    return (SET_A, SET_B)[(s + layer) % 2]


INPUTS = ["x", "norm_g", "sb_w_in", "sb_w_out", "sc_conv_w", "sc_conv_b", "sc_w_in", "sc_w_out"]


def kernel(**inputs):
    import concourse.bacc as bacc
    from concourse.bass_utils import run_bass_kernel_spmd

    nc = bacc.Bacc("TRN2", target_bir_lowering=False, num_devices=1)
    arrays, args = {}, []
    for name in INPUTS:
        a = np.ascontiguousarray(inputs[name])
        arrays[f"in_{name}"] = a
        args.append(nc.dram_tensor(f"in_{name}", a.shape, mybir.dt.from_np(a.dtype), kind="ExternalInput").ap())
    args.append(nc.dram_tensor("x1_dram", (SEQ, D), F32, kind="Internal").ap())
    args.append(nc.dram_tensor("out_dram", (1, SEQ, D), F32, kind="ExternalOutput").ap())
    trunk(nc, *args)
    r = run_bass_kernel_spmd(nc, [arrays], core_ids=[0])
    return r.results[0]["out_dram"]
```

```python
from contextlib import ExitStack

import numpy as np

import concourse.bass as bass
import concourse.mybir as mybir
from concourse.alu_op_type import AluOpType as ALU

ACT = mybir.ActivationFunctionType
F32 = mybir.dt.float32
F32R = mybir.dt.float32r

P = 128
SEQ = 512
D = 2048
KT = D // P
TB = SEQ // P
EPS = 1e-6
MASKED = -1e30
QSCALE = float(P) ** -0.5

PIECE = 512
PIECES = 16
STEPS = KT // 4
WSLOTS = 4
RAWSLOTS = 2

IN0 = 0
OUT0 = IN0 + KT * PIECES
IN1 = OUT0 + STEPS * PIECES
OUT1 = IN1 + KT * PIECES

Z_AT = {3: 0, 2: 512, 0: 896, 1: 1024}
Z_COLS = 1280
AT_PSUM = [0, 512, 1024, 1280]
AT_SBUF = [0, 512, 896, 1152]
AT_FROM = [0, 128, 256, 256]
AT_COLS = 1408

BANKS = [0, 1, 6, 7]
BANK_Z = 2
BANK_O = 5
BANK_RS = 5

G_AT, CW_AT, CB_AT, PARAMS = 0, 2 * KT, 5 * KT, 6 * KT


def wait(engine, semaphore, value):
    if isinstance(value, int) and value <= 0:
        return
    engine.wait_ge(semaphore, value)


def trunk(nc, x_t, params, sb_w_in, sb_w_out, sc_w_in, sc_w_out, x1_t, out_t):
    x_v, x1_v, out_v = (a.rearrange("(k p) t -> p k t", p=P) for a in (x_t, x1_t, out_t))
    w_in = [w[0].rearrange("(k p) n -> p k n", p=P) for w in (sb_w_in, sc_w_in)]
    w_out = [w[0].rearrange("(k p) n -> p k n", p=P) for w in (sb_w_out, sc_w_out)]

    with ExitStack() as ctx:
        def sb(name, shape, dt=F32):
            return ctx.enter_context(nc.sbuf_tensor(name, shape, dt))

        def sem(name):
            return ctx.enter_context(nc.semaphore(name))

        xh = sb("x_high", [P, KT, SEQ], F32R)
        xl = sb("x_low", [P, KT, SEQ], F32R)
        yh = sb("y_high", [P, KT, SEQ], F32R)
        yl = sb("y_low", [P, KT, SEQ], F32R)
        raw = sb("w_raw", [P, RAWSLOTS, 2 * PIECE])
        wh = sb("w_high", [P, WSLOTS, PIECE], F32R)
        wl = sb("w_low", [P, WSLOTS, PIECE], F32R)
        stage0 = sb("stage0", [P, 2 * Z_COLS])
        stage1 = sb("stage1", [P, 4 * SEQ])
        qh, ql, kh, kl, vh, vl = (sb(n, [P, SEQ], F32R) for n in ("q_high", "q_low", "k_high", "k_low", "v_high", "v_low"))
        ah = sb("a_high", [P, AT_COLS], F32R)
        al = sb("a_low", [P, AT_COLS], F32R)
        ident = sb("ident", [P, P])
        ones = sb("ones", [P, P])
        mask = sb("mask", [P, 3, P])
        rs_b = sb("rs_b", [P, SEQ])
        rs2_b = sb("rs2_b", [P, SEQ])
        diag = sb("diag", [P, SEQ])
        sq = sb("sq", [P, 2, SEQ])
        prm = sb("prm", [P, PARAMS])
        rsn = sb("rsn", [P, 5, TB])
        ps = ctx.enter_context(nc.psum_tensor("ps", [P, 8, 512], F32))

        acc = rs2_b
        stage = [stage0[:, 0:1024], stage0[:, 1024:2048], stage1[:, 0:1024], stage1[:, 1024:2048]]
        ta = stage0[:, 0:Z_COLS]
        tb_ = stage0[:, Z_COLS:2 * Z_COLS]
        f = stage1[:, 0:SEQ]
        fv = stage1[:, SEQ:2 * SEQ]
        gs = stage1[:, 2 * SEQ:3 * SEQ]
        ge = stage1[:, 3 * SEQ:4 * SEQ]
        cu = stage0[:, 0:SEQ + 2]
        t1 = stage0[:, SEQ + 2:2 * SEQ + 2]
        cv = stage0[:, 2 * SEQ + 2:3 * SEQ + 2]
        bb = stage0[:, 3 * SEQ + 2:4 * SEQ + 2]
        res = [fv, stage0[:, Z_COLS:Z_COLS + SEQ], stage0[:, Z_COLS + SEQ:Z_COLS + 2 * SEQ], stage0[:, 0:SEQ]]
        z = ps[:, BANK_Z:BANK_Z + 3, :].rearrange("p b n -> p (b n)")

        landed = [sem(f"landed{i}") for i in range(RAWSLOTS)]
        hi_done, lo_done, piece_used = sem("hi_done"), sem("lo_done"), sem("piece_used")
        params_landed, zeroed, consts = sem("params_landed"), sem("zeroed"), sem("consts")
        x_landed = [sem(f"x_landed{i}") for i in range(4)]
        r_landed = [sem(f"r_landed{i}") for i in range(4)]
        stored = [sem(f"stored{i}") for i in range(4)]
        x_hi, x_lo = sem("x_hi"), sem("x_lo")
        squared, summed, cleared = sem("squared"), sem("summed"), sem("cleared")
        ssq_done, rs_steps, rs_root, rs_sum = sem("ssq_done"), sem("rs_steps"), sem("rs_root"), sem("rs_sum")
        proj_read = sem("proj_read")
        qk_hi, qk_lo = sem("qk_hi"), sem("qk_lo")
        v_t, v_hi, v_lo = sem("v_t"), sem("v_hi"), sem("v_lo")
        z_done, z_masked, softplus, logits = sem("z_done"), sem("z_masked"), sem("softplus"), sem("logits")
        a_done, a_t, a_hi, a_lo = sem("a_done"), sem("a_t"), sem("a_hi"), sem("a_lo")
        gate_act, gate_steps, conv_steps = sem("gate_act"), sem("gate_steps"), sem("conv_steps")
        av_done, y_read, y_hi, y_lo = sem("av_done"), sem("y_read"), sem("y_hi"), sem("y_lo")
        x1_ready = sem("x1_ready")
        block = ctx.enter_context(nc.Block())

        def raw_piece(slot, out):
            load = raw[:, slot // 2 % RAWSLOTS, :]
            if out:
                return load.rearrange("p (k n) -> p k n", k=4)[:, :, P * (slot % 2):P * (slot % 2 + 1)]
            return load[:, PIECE * (slot % 2):PIECE * (slot % 2 + 1)].rearrange("p (k n) -> p k n", k=4)

        def split_piece(w, slot):
            return w[:, slot % WSLOTS, :].rearrange("p (k n) -> p k n", k=4)

        RS_STEPS = 8

        @block.sync
        def _(sp):
            def load(n0, part, src):
                wait(sp, lo_done, n0 + 2 * part - 2)
                sp.dma_start(raw[:, part % RAWSLOTS, :].rearrange("p (k n) -> p k n", n=src.shape[-1]), src)\
                  .then_inc(landed[part % RAWSLOTS], 16)

            def in_loads(layer, n0, tile, parts=range(8)):
                for part in parts:
                    col = (part // 2) * D + tile * P
                    load(n0, part, w_in[layer][:, 8 * (part % 2):8 * (part % 2) + 8, bass.ds(col, P)])

            def x_load(i):
                wait(sp, squared, 2 * i - 6)
                wait(sp, x_lo, 2 * i - 6)
                sp.dma_start(stage[i % 4].rearrange("p (k n) -> p k n", k=2), x_v[:, 2 * i:2 * i + 2, :]).then_inc(x_landed[i % 4], 16)

            def residual_load(layer, tile):
                if tile >= 4:
                    sp.wait_ge(stored[tile % 4], 16 * (STEPS * layer + tile // 4))
                    if layer == 0:
                        sp.wait_ge(x_lo, KT + tile - 3)
                        sp.wait_ge(squared, KT + tile - 3)
                elif layer == 0:
                    sp.wait_ge((v_t, a_done, a_done, a_t)[tile], KT)
                else:
                    sp.wait_ge(stored[tile], 16 * STEPS)
                    sp.wait_ge(y_lo, 2 * KT)
                sp.dma_start(res[tile % 4], (x_v, x1_v)[layer][:, tile, :]).then_inc(r_landed[tile % 4], 16)

            def store(layer, tile):
                sp.wait_ge(x1_ready, KT * layer + tile + 1)
                sp.dma_start((x1_v, out_v)[layer][:, tile, :], res[tile % 4]).then_inc(stored[tile % 4], 16)

            def beside(layer, part):
                step, part = divmod(part, 8)
                for i in range(4):
                    if step and part == 2 + i // 2:
                        store(layer, 4 * step - 4 + i)
                    if step < STEPS and part == 5:
                        residual_load(layer, 4 * step + i)

            def out_phase(layer, n0):
                for part in range(8 * STEPS):
                    kt, col = 4 * (part % 8 // 2), 4 * P * (part // 8) + 2 * P * (part % 2)
                    load(n0 + PIECES * (part // 8), part % 8, w_out[layer][:, kt:kt + 4, col:col + 2 * P])
                    beside(layer, part)

            sp.dma_start(prm[:, :], params).then_inc(params_landed, 16)
            x_load(0)
            in_loads(0, IN0, 0, [0])
            for i in range(1, 4):
                x_load(i)
            in_loads(0, IN0, 0, [1])
            for i in range(4, 8):
                x_load(i)
            in_loads(0, IN0, 0, range(2, 8))
            with sp.Fori(1, KT) as h:
                in_loads(0, IN0 + PIECES * h, h)
            out_phase(0, OUT0)
            for part in range(8):
                in_loads(1, IN1, 0, [part])
                beside(0, 8 * STEPS + part)
            with sp.Fori(1, KT) as t:
                in_loads(1, IN1 + PIECES * t, t)
            out_phase(1, OUT1)
            for part in range(8 * STEPS, 8 * STEPS + 4):
                beside(1, part)
            for i in range(4):
                sp.wait_ge(stored[i], 2 * 16 * STEPS)

        @block.gpsimd
        def _(pool):
            pool.memset(ident[:, :], 0.0).then_inc(zeroed, 1)
            pool.memset(mask[:, :, :], 0.0).then_inc(zeroed, 1)
            pool.memset(ones[:, :], 1.0).then_inc(consts, 1)
            pool.wait_ge(zeroed, 2)
            pool.affine_select(out=ident[:, :], in_=ident[:, :], compare_op=ALU.not_equal, fill=1.0, base=0,
                               pattern=[[-1, P]], channel_multiplier=1).then_inc(consts, 1)
            pool.affine_select(out=mask[:, :, :], in_=mask[:, :, :], compare_op=ALU.is_ge, fill=MASKED, base=-1,
                               pattern=[[0, 3], [-1, P]], channel_multiplier=1).then_inc(consts, 1)
            pool.memset(ah[:, AT_SBUF[3]:AT_SBUF[3] + P].bitcast(F32), 0.0).then_inc(consts, 1)
            pool.memset(al[:, AT_SBUF[3]:AT_SBUF[3] + P].bitcast(F32), 0.0).then_inc(consts, 1)
            for kt in range(KT):
                if kt % 2 == 0:
                    pool.wait_ge(x_landed[kt // 2 % 4], 16 * (kt // 8 + 1))
                wait(pool, summed, kt - 1)
                x = stage[kt // 2 % 4][:, SEQ * (kt % 2):SEQ * (kt % 2 + 1)]
                pool.tensor_tensor(sq[:, kt % 2, :], x, x, ALU.mult).then_inc(squared, 1)

        @block.scalar
        def _(act):
            def hi(n0, slot, out=False):
                load = slot // 2
                if slot % 2 == 0:
                    act.wait_ge(landed[load % RAWSLOTS], landed_value(n0, load))
                wait(act, piece_used, n0 + slot - WSLOTS + 1)
                nc.scalar.copy(split_piece(wh, slot), raw_piece(slot, out)).then_inc(hi_done, 1)

            def landed_value(n0, load):
                return n0 * 4 + 16 * (load // 2 + 1)

            def softplus_tail(j):
                act.wait_ge(z_masked, j + 1)
                nc.scalar.activation(ta, z[:, 0:Z_COLS], ACT.Abs).then_inc(softplus, 1)
                act.wait_ge(softplus, 3 * j + 1)
                nc.scalar.activation(ta, ta, ACT.Exp, scale=-1.0).then_inc(softplus, 1)
                act.wait_ge(softplus, 3 * j + 2)
                nc.scalar.activation(ta, ta, ACT.Ln, bias=1.0).then_inc(softplus, 1)

            def weights(j):
                act.wait_ge(logits, 3 * j + 3)
                nc.scalar.activation(ta, tb_, ACT.Exp).then_inc(a_done, 1)

            def gate_exp(j):
                act.wait_ge(proj_read, 4 * j + 4)
                nc.scalar.activation(ge, gs, ACT.Exp, scale=-1.0).then_inc(gate_act, 1)

            def v_high(j):
                act.wait_ge(v_t, j + 1)
                nc.scalar.copy(vh[:, :], ps[:, BANK_O, :]).then_inc(v_hi, 1)

            def q_high(h):
                act.wait_ge(proj_read, 4 * h + 1)
                nc.scalar.copy(qh[:, :], f).then_inc(qk_hi, 1)

            def k_high(h):
                act.wait_ge(proj_read, 4 * h + 2)
                nc.scalar.copy(kh[:, :], f).then_inc(qk_hi, 1)

            def a_high(j):
                act.wait_ge(a_t, j + 1)
                nc.scalar.copy(ah[:, 0:896], z[:, 0:896])
                nc.scalar.copy(ah[:, 896:1152], z[:, 1024:1280])
                nc.scalar.copy(ah[:, 1280:1408], z[:, 1280:1408]).then_inc(a_hi, 1)

            def y_high(j, i):
                act.wait_ge(y_read, i + 1)
                nc.scalar.copy(yh[:, bass.ds(j, 1), :].rearrange("p a n -> p (a n)"), f).then_inc(y_hi, 1)

            def x_high(kt):
                if kt % 2 == 0:
                    act.wait_ge(x_landed[kt // 2 % 4], 16 * (kt // 8 + 1))
                x = stage[kt // 2 % 4][:, SEQ * (kt % 2):SEQ * (kt % 2 + 1)]
                nc.scalar.activation(xh[:, kt, :], x, ACT.Copy, scale=prm[:, G_AT + kt:G_AT + kt + 1]).then_inc(x_hi, 1)

            def x1_high(m, i):
                act.wait_ge(x1_ready, m + 1)
                nc.scalar.activation(xh[:, bass.ds(m, 1), :].rearrange("p a n -> p (a n)"), res[i], ACT.Copy,
                                     scale=prm[:, bass.ds(G_AT + KT + m, 1)]).then_inc(x_hi, 1)
                act.wait_ge(summed, KT + m - 1)
                nc.scalar.activation(sq[:, i % 2, :], res[i], ACT.Square).then_inc(squared, 1)

            def root(layer):
                act.wait_ge(rs_steps, RS_STEPS * layer + 1)
                nc.scalar.activation(rsn[:, 1, :], rsn[:, 0, :], ACT.Sqrt).then_inc(rs_root, 1)

            act.wait_ge(params_landed, 16)
            for slot in range(PIECES):
                if slot < 4:
                    for kt in range(4 * slot, 4 * slot + 4):
                        x_high(kt)
                hi(IN0, slot)
                if slot == 9:
                    root(0)
                if slot == 12:
                    q_high(0)
                if slot == 13:
                    k_high(0)

            def attend(slot, j, i):
                if slot == 0:
                    softplus_tail(j)
                if slot == 4:
                    gate_exp(j)
                if slot == 5:
                    weights(j)
                if slot == 6:
                    v_high(j)
                if slot == 8:
                    a_high(j)
                if slot == 12:
                    y_high(j, i)

            with act.Fori(1, KT) as h:
                for slot in range(PIECES):
                    hi(IN0 + PIECES * h, slot)
                    if slot == 7:
                        q_high(h)
                    if slot == 11:
                        k_high(h)
                    attend(slot, h - 1, h - 1)

            for slot in range(PIECES):
                hi(OUT0, slot, out=True)
                attend(slot, KT - 1, KT - 1)
            with act.Fori(1, STEPS) as s:
                for slot in range(PIECES):
                    hi(OUT0 + PIECES * s, slot, out=True)
                    if slot < 4:
                        x1_high(4 * s - 4 + slot, slot)

            def gate_silu(t):
                act.wait_ge(proj_read, 4 * (KT + t) + 4)
                nc.scalar.activation(ge, gs, ACT.Silu).then_inc(gate_act, 1)

            for slot in range(PIECES):
                hi(IN1, slot)
                if slot < 4:
                    x1_high(KT - 4 + slot, slot)
                if slot == 7:
                    root(1)
            with act.Fori(1, KT) as t:
                for slot in range(PIECES):
                    hi(IN1 + PIECES * t, slot)
                    if slot == 3:
                        gate_silu(t - 1)
                    if slot == 4:
                        y_high(t - 1, KT + t - 1)
            for slot in range(PIECES):
                hi(OUT1, slot, out=True)
                if slot == 3:
                    gate_silu(KT - 1)
                if slot == 4:
                    y_high(KT - 1, 2 * KT - 1)
            with act.Fori(1, STEPS) as s:
                for slot in range(PIECES):
                    hi(OUT1 + PIECES * s, slot, out=True)

        @block.vector
        def _(dve):
            def lo(n0, slot, out=False):
                dve.wait_ge(hi_done, n0 + slot + 1)
                nc.vector.tensor_tensor(split_piece(wl, slot), raw_piece(slot, out), split_piece(wh, slot).bitcast(F32),
                                        ALU.subtract).then_inc(lo_done, 1)

            def clear_sum(n):
                nc.vector.memset(acc[:, :], 0.0).then_inc(cleared, 1)
                dve.wait_ge(cleared, n)

            def add_squares(n, i):
                dve.wait_ge(squared, n + 1)
                wait(dve, summed, n)
                nc.vector.tensor_tensor(acc[:, :], acc[:, :], sq[:, i, :], ALU.add).then_inc(summed, 1)

            def x_low(kt):
                dve.wait_ge(x_hi, kt + 1)
                x = stage[kt // 2 % 4][:, SEQ * (kt % 2):SEQ * (kt % 2 + 1)]
                nc.vector.scalar_tensor_tensor(xl[:, kt, :], x, prm[:, G_AT + kt:G_AT + kt + 1], xh[:, kt, :].bitcast(F32),
                                               ALU.mult, ALU.subtract).then_inc(x_lo, 1)

            def residual(n1, i, rounds):
                dve.wait_ge(piece_used, n1 - 3 + i)
                dve.wait_ge(r_landed[i], 16 * rounds)
                nc.vector.tensor_tensor(res[i], ps[:, BANKS[i], :], res[i], ALU.add).then_inc(x1_ready, 1)

            def x1_low(m, i):
                dve.wait_ge(x_hi, KT + m + 1)
                nc.vector.scalar_tensor_tensor(xl[:, bass.ds(m, 1), :].rearrange("p a n -> p (a n)"), res[i],
                                               prm[:, bass.ds(G_AT + KT + m, 1)],
                                               xh[:, bass.ds(m, 1), :].rearrange("p a n -> p (a n)").bitcast(F32),
                                               ALU.mult, ALU.subtract).then_inc(x_lo, 1)

            def x1_split(slot, n1, m0, rounds):
                if slot < 4:
                    residual(n1, slot, rounds)
                if 0 < slot < 5:
                    x1_low(m0 + slot - 1, slot - 1)
                    add_squares(KT + m0 + slot - 1, (slot - 1) % 2)

            def inverse_rms(layer):
                n = RS_STEPS * layer
                tot, root, inv, tmp, fac = (rsn[:, i, :] for i in range(5))
                dve.wait_ge(ssq_done, layer + 1)
                nc.vector.tensor_scalar(tot, ps[:, BANK_RS, 0:TB], 1.0 / D, EPS, ALU.mult, ALU.add).then_inc(rs_steps, 1)
                dve.wait_ge(rs_root, layer + 1)
                nc.vector.reciprocal(inv, root).then_inc(rs_steps, 1)
                dve.wait_ge(rs_steps, n + 2)
                nc.vector.tensor_tensor(tmp, inv, inv, ALU.mult).then_inc(rs_steps, 1)
                dve.wait_ge(rs_steps, n + 3)
                nc.vector.tensor_tensor(fac, tmp, tot, ALU.mult).then_inc(rs_steps, 1)
                dve.wait_ge(rs_steps, n + 4)
                nc.vector.tensor_scalar(fac, fac, -0.5, 1.5, ALU.mult, ALU.add).then_inc(rs_steps, 1)
                dve.wait_ge(rs_steps, n + 5)
                nc.vector.tensor_tensor(inv, inv, fac, ALU.mult).then_inc(rs_steps, 1)
                dve.wait_ge(rs_steps, n + 6)
                for t in range(TB):
                    last = nc.vector.tensor_scalar(diag[:, t * P:(t + 1) * P], ident[:, :], inv[:, t:t + 1], None, ALU.mult)
                last.then_inc(rs_steps, 1)

            def spread_rms(layer):
                n = RS_STEPS * layer
                dve.wait_ge(rs_sum, layer + 1)
                nc.vector.tensor_copy(rs_b[:, :], ps[:, BANK_RS, :]).then_inc(rs_steps, 1)
                dve.wait_ge(rs_steps, n + 8)
                if layer == 1:
                    nc.vector.tensor_tensor(rs2_b[:, :], rs_b[:, :], rs_b[:, :], ALU.mult).then_inc(rs_steps, 1)
                    dve.wait_ge(rs_steps, n + 9)

            def q_read(h):
                dve.wait_ge(piece_used, PIECES * h + 4)
                wait(dve, y_lo, h - 1)
                nc.vector.scalar_tensor_tensor(f, ps[:, BANKS[0], :], QSCALE, rs_b[:, :], ALU.mult, ALU.mult).then_inc(proj_read, 1)

            def q_low(h):
                dve.wait_ge(qk_hi, 2 * h + 1)
                nc.vector.tensor_tensor(ql[:, :], f, qh[:, :].bitcast(F32), ALU.subtract).then_inc(qk_lo, 1)

            def k_read(h):
                dve.wait_ge(piece_used, PIECES * h + 8)
                dve.wait_ge(qk_lo, 2 * h + 1)
                nc.vector.tensor_tensor(f, ps[:, BANKS[1], :], rs_b[:, :], ALU.mult).then_inc(proj_read, 1)

            def k_low(h):
                dve.wait_ge(qk_hi, 2 * h + 2)
                nc.vector.tensor_tensor(kl[:, :], f, kh[:, :].bitcast(F32), ALU.subtract).then_inc(qk_lo, 1)

            def v_read(h):
                dve.wait_ge(piece_used, PIECES * h + 12)
                nc.vector.tensor_tensor(fv, ps[:, BANKS[2], :], rs_b[:, :], ALU.mult).then_inc(proj_read, 1)

            def g_read(j):
                dve.wait_ge(piece_used, PIECES * j + 16)
                wait(dve, y_read, j)
                nc.vector.tensor_tensor(gs, ps[:, BANKS[3], :], rs_b[:, :], ALU.mult).then_inc(proj_read, 1)

            def mask_z(h):
                dve.wait_ge(z_done, h + 1)
                d3 = z[:, 384:1536].rearrange("p (a n) -> p a n", n=384)[:, :, 0:P]
                nc.vector.tensor_tensor(d3, d3, mask[:, :, :], ALU.add)
                d0 = z[:, Z_AT[0]:Z_AT[0] + P]
                nc.vector.tensor_tensor(d0, d0, mask[:, 0, :], ALU.add).then_inc(z_masked, 1)

            def softplus_sum(j):
                dve.wait_ge(softplus, 3 * j + 3)
                nc.vector.scalar_tensor_tensor(tb_, z[:, 0:Z_COLS], 0.0, ta, ALU.max, ALU.add).then_inc(logits, 1)

            def cumulate(j, blocks):
                if 3 in blocks:
                    dve.wait_ge(logits, 3 * j + 1)
                for i in blocks:
                    c0, n = Z_AT[i], P * (i + 1)
                    term = tb_[:, c0:c0 + n][:, ::-1]
                    last = nc.vector.tensor_tensor_scan(ta[:, c0:c0 + n][:, ::-1], term, term, 0.0, ALU.add, ALU.max)
                if 1 in blocks:
                    last.then_inc(logits, 1)

            def subtract(j):
                dve.wait_ge(logits, 3 * j + 2)
                nc.vector.tensor_tensor(tb_, z[:, 0:Z_COLS], ta, ALU.subtract).then_inc(logits, 1)

            def silu(j):
                dve.wait_ge(gate_act, j + 1)
                nc.vector.tensor_scalar(ge, ge, 1.0, None, ALU.add).then_inc(gate_steps, 1)
                dve.wait_ge(gate_steps, 3 * j + 1)
                nc.vector.reciprocal(ge, ge).then_inc(gate_steps, 1)
                dve.wait_ge(gate_steps, 3 * j + 2)
                nc.vector.tensor_tensor(gs, gs, ge, ALU.mult).then_inc(gate_steps, 1)

            def v_low(j):
                dve.wait_ge(v_hi, j + 1)
                nc.vector.tensor_tensor(vl[:, :], ps[:, BANK_O, :], vh[:, :].bitcast(F32), ALU.subtract).then_inc(v_lo, 1)

            def a_low(j):
                dve.wait_ge(a_hi, j + 1)
                nc.vector.tensor_tensor(al[:, 0:896], z[:, 0:896], ah[:, 0:896].bitcast(F32), ALU.subtract)
                nc.vector.tensor_tensor(al[:, 896:1152], z[:, 1024:1280], ah[:, 896:1152].bitcast(F32), ALU.subtract)
                nc.vector.tensor_tensor(al[:, 1280:1408], z[:, 1280:1408], ah[:, 1280:1408].bitcast(F32),
                                        ALU.subtract).then_inc(a_lo, 1)

            def o_read(j):
                dve.wait_ge(av_done, j + 1)
                dve.wait_ge(gate_steps, 3 * j + 3)
                dve.wait_ge(qk_lo, 2 * KT if isinstance(j, int) and j == KT - 1 else 2 * j + 4)
                nc.vector.tensor_tensor(f, ps[:, BANK_O, :], gs, ALU.mult).then_inc(y_read, 1)

            def y_low(j, i):
                dve.wait_ge(y_hi, i + 1)
                nc.vector.tensor_tensor(yl[:, bass.ds(j, 1), :].rearrange("p a n -> p (a n)"), f,
                                        yh[:, bass.ds(j, 1), :].rearrange("p a n -> p (a n)").bitcast(F32),
                                        ALU.subtract).then_inc(y_lo, 1)

            def attend(slot, j, i):
                if slot == 1:
                    softplus_sum(j)
                if slot == 2:
                    cumulate(j, (3,))
                if slot == 3:
                    g_read(j)
                    cumulate(j, (2, 0, 1))
                if slot == 4:
                    subtract(j)
                if slot == 5:
                    silu(j)
                if slot == 6:
                    v_low(j)
                if slot == 9:
                    a_low(j)
                if slot == 12:
                    o_read(j)
                if slot == 13:
                    y_low(j, i)

            def project(slot, h):
                if slot == 7:
                    q_read(h)
                if slot == 8:
                    q_low(h)
                if slot == 11:
                    k_read(h)
                if slot == 12:
                    k_low(h)
                if slot == 15:
                    v_read(h)
                    mask_z(h)

            clear_sum(1)
            dve.wait_ge(params_landed, 16)
            for slot in range(4):
                for kt in range(4 * slot, 4 * slot + 4):
                    x_low(kt)
                    if kt >= 4:
                        add_squares(kt - 4, kt % 2)
                lo(IN0, slot)
            for slot in range(4, PIECES):
                lo(IN0, slot)
                if slot < 8:
                    add_squares(KT - 8 + slot, slot % 2)
                if slot == 9:
                    dve.wait_ge(consts, 5)
                    inverse_rms(0)
                if slot == 12:
                    spread_rms(0)
                    q_read(0)
                if slot == 13:
                    q_low(0)
                    k_read(0)
                if slot == 14:
                    k_low(0)
                if slot == 15:
                    v_read(0)
                    mask_z(0)
            with dve.Fori(1, KT) as h:
                for slot in range(PIECES):
                    lo(IN0 + PIECES * h, slot)
                    project(slot, h)
                    attend(slot, h - 1, h - 1)

            for slot in range(PIECES):
                lo(OUT0, slot, out=True)
                attend(slot, KT - 1, KT - 1)
            clear_sum(2)
            with dve.Fori(1, STEPS) as s:
                for slot in range(PIECES):
                    lo(OUT0 + PIECES * s, slot, out=True)
                    x1_split(slot, OUT0 + PIECES * s, 4 * s - 4, s)

            def b_read(t):
                dve.wait_ge(piece_used, IN1 + PIECES * t + 4)
                dve.wait_ge(conv_steps, 4 * t + 1)
                nc.vector.tensor_tensor(bb, ps[:, BANKS[0], :], rs_b[:, :], ALU.mult).then_inc(proj_read, 1)

            def c_read(t):
                dve.wait_ge(piece_used, IN1 + PIECES * t + 8)
                nc.vector.tensor_tensor(t1, ps[:, BANKS[1], :], rs2_b[:, :], ALU.mult).then_inc(proj_read, 1)

            def u_read(t):
                dve.wait_ge(piece_used, IN1 + PIECES * t + 12)
                dve.wait_ge(proj_read, 4 * (KT + t) + 2)
                nc.vector.tensor_tensor(cu[:, 2:], ps[:, BANKS[2], :], t1, ALU.mult).then_inc(proj_read, 1)

            def conv(t):
                def tap(i):
                    return prm[:, bass.ds(CW_AT + KT * i + t, 1)]
                dve.wait_ge(proj_read, 4 * (KT + t) + 3)
                dve.wait_ge(y_read, KT + t)
                nc.vector.tensor_scalar(cv, cu[:, 2:], tap(2), prm[:, bass.ds(CB_AT + t, 1)], ALU.mult, ALU.add).then_inc(conv_steps, 1)
                dve.wait_ge(conv_steps, 4 * t + 2)
                nc.vector.scalar_tensor_tensor(cv, cu[:, 1:SEQ + 1], tap(1), cv, ALU.mult, ALU.add).then_inc(conv_steps, 1)
                dve.wait_ge(conv_steps, 4 * t + 3)
                nc.vector.scalar_tensor_tensor(cv, cu[:, 0:SEQ], tap(0), cv, ALU.mult, ALU.add).then_inc(conv_steps, 1)
                dve.wait_ge(conv_steps, 4 * t + 4)
                nc.vector.tensor_tensor(cv, cv, bb, ALU.mult).then_inc(conv_steps, 1)

            def gate_read(t):
                dve.wait_ge(piece_used, IN1 + PIECES * t + 16)
                nc.vector.tensor_tensor(gs, ps[:, BANKS[3], :], rs_b[:, :], ALU.mult).then_inc(proj_read, 1)

            def mix(t):
                dve.wait_ge(gate_act, KT + t + 1)
                dve.wait_ge(conv_steps, 4 * t + 5)
                dve.wait_ge(y_lo, KT + t)
                nc.vector.tensor_tensor(f, cv, ge, ALU.mult).then_inc(y_read, 1)

            def branch(slot, t):
                if slot == 7:
                    b_read(t)
                if slot == 11:
                    c_read(t)
                if slot == 15:
                    u_read(t)

            def branch_end(slot, t):
                if slot == 0:
                    conv(t)
                if slot == 3:
                    gate_read(t)
                if slot == 4:
                    mix(t)
                if slot == 5:
                    y_low(t, KT + t)

            for slot in range(PIECES):
                lo(IN1, slot)
                x1_split(slot, IN1, KT - 4, STEPS)
                if slot == 7:
                    inverse_rms(1)
                if slot == 10:
                    spread_rms(1)
                    for i in range(1, 4):
                        dve.wait_ge(stored[i], 16 * STEPS)
                    nc.vector.memset(cu[:, 0:2], 0.0).then_inc(conv_steps, 1)
                    dve.wait_ge(conv_steps, 1)
                    b_read(0)
                if slot == 11:
                    c_read(0)
                if slot == 15:
                    u_read(0)
            with dve.Fori(1, KT) as t:
                for slot in range(PIECES):
                    lo(IN1 + PIECES * t, slot)
                    branch_end(slot, t - 1)
                    branch(slot, t)
            for slot in range(PIECES):
                lo(OUT1, slot, out=True)
                branch_end(slot, KT - 1)
            with dve.Fori(1, STEPS) as s:
                for slot in range(PIECES):
                    lo(OUT1 + PIECES * s, slot, out=True)
                    if slot < 4:
                        residual(OUT1 + PIECES * s, slot, STEPS + s)
            for i in range(4):
                residual(OUT1 + PIECES * STEPS, i, 2 * STEPS)

        @block.tensor
        def _(pe):
            def three(acc, sh, sl, mh, ml, start, stop):
                nc.tensor.matmul(acc, sh, mh, start=start, stop=False)
                nc.tensor.matmul(acc, sh, ml, start=False, stop=False)
                return nc.tensor.matmul(acc, sl, mh, start=False, stop=stop)

            def piece(n0, slot, mh, ml, split=None, behind=0, out=False):
                pe.wait_ge(lo_done, n0 + slot + 1)
                tile, quarter = (slot % 4, slot // 4) if out else (slot // 4, slot % 4)
                for i in range(4):
                    kt = 4 * quarter + i
                    w = slice(i * P, (i + 1) * P)
                    if split is not None:
                        pe.wait_ge(split, behind + kt + 1)
                    last = three(ps[:, BANKS[tile], :], wh[:, slot % WSLOTS, w], wl[:, slot % WSLOTS, w],
                                 mh[:, kt, :], ml[:, kt, :], kt == 0, kt == KT - 1)
                last.then_inc(piece_used, 1)

            def sum_squares(layer):
                pe.wait_ge(summed, KT * (layer + 1))
                for t in range(TB):
                    last = nc.tensor.matmul(ps[:, BANK_RS, t:t + 1], acc[:, t * P:(t + 1) * P], ones[:, 0:1], start=True, stop=True)
                last.then_inc(ssq_done, 1)

            def spread(layer):
                pe.wait_ge(rs_steps, RS_STEPS * layer + 7)
                nc.tensor.matmul(ps[:, BANK_RS, :], ones[:, :], diag[:, :], start=True, stop=True).then_inc(rs_sum, 1)

            def logits_of(h):
                pe.wait_ge(qk_lo, 2 * h + 2)
                for i in (3, 2, 0, 1):
                    q, n = slice(i * P, (i + 1) * P), P * (i + 1)
                    last = three(z[:, Z_AT[i]:Z_AT[i] + n], qh[:, q], ql[:, q], kh[:, 0:n], kl[:, 0:n], True, True)
                last.then_inc(z_done, 1)

            def v_transpose(h):
                pe.wait_ge(proj_read, 4 * h + 3)
                wait(pe, y_read, h)
                for t in range(TB):
                    last = nc.tensor.transpose(ps[:, BANK_O, t * P:(t + 1) * P], fv[:, t * P:(t + 1) * P], ident[:, :])
                last.then_inc(v_t, 1)

            def a_transpose(j):
                pe.wait_ge(a_done, j + 1)
                for kb in range(TB):
                    for i in range(kb, TB):
                        last = nc.tensor.transpose(z[:, AT_PSUM[kb] + P * (i - kb):AT_PSUM[kb] + P * (i - kb + 1)],
                                                   ta[:, Z_AT[i] + P * kb:Z_AT[i] + P * (kb + 1)], ident[:, :])
                last.then_inc(a_t, 1)

            def output_of(j):
                pe.wait_ge(v_lo, j + 1)
                pe.wait_ge(a_lo, j + 1)
                for kb in range(TB):
                    q0, c0, v = AT_FROM[kb], AT_SBUF[kb], slice(kb * P, (kb + 1) * P)
                    n = SEQ - q0
                    last = three(ps[:, BANK_O, q0:SEQ], vh[:, v], vl[:, v], ah[:, c0:c0 + n], al[:, c0:c0 + n], kb == 0, kb == TB - 1)
                last.then_inc(av_done, 1)

            pe.wait_ge(consts, 5)
            for slot in range(PIECES):
                piece(IN0, slot, xh, xl, x_lo if slot < 4 else None)
                if slot == 8:
                    sum_squares(0)
                if slot == 10:
                    spread(0)
                if slot == 13:
                    logits_of(0)
            v_transpose(0)
            with pe.Fori(1, KT) as h:
                for slot in range(PIECES):
                    if slot == 4:
                        a_transpose(h - 1)
                    if slot == 8:
                        output_of(h - 1)
                    if slot == 12:
                        logits_of(h)
                    if slot % 4 == 0:
                        pe.wait_ge(proj_read, 4 * h - 3 + slot // 4)
                    piece(IN0 + PIECES * h, slot, xh, xl)
                v_transpose(h)
            def out_phase(layer, n0):
                for slot in range(PIECES):
                    if slot == 0:
                        pe.wait_ge(y_lo, KT * layer + KT - 1)
                    if layer == 0 and slot == 4:
                        a_transpose(KT - 1)
                    if layer == 0 and slot == 8:
                        output_of(KT - 1)
                    if slot < 4:
                        pe.wait_ge(proj_read, 4 * KT * (layer + 1) - 3 + slot)
                    if slot == 12:
                        pe.wait_ge(y_lo, KT * (layer + 1))
                    piece(n0, slot, yh, yl, out=True)
                with pe.Fori(1, STEPS) as s:
                    for slot in range(PIECES):
                        if slot < 4:
                            pe.wait_ge(x1_ready, KT * layer + 4 * s - 3 + slot)
                        piece(n0 + PIECES * s, slot, yh, yl, out=True)

            out_phase(0, OUT0)
            for slot in range(PIECES):
                if slot % 4 == 0:
                    pe.wait_ge(x1_ready, KT - 3 + slot // 4)
                piece(IN1, slot, xh, xl, x_lo if slot < 4 else None, KT)
                if slot == 6:
                    sum_squares(1)
                if slot == 8:
                    spread(1)
            with pe.Fori(1, KT) as t:
                for slot in range(PIECES):
                    if slot % 4 == 0:
                        pe.wait_ge(proj_read, 4 * (KT + t) - 3 + slot // 4)
                    piece(IN1 + PIECES * t, slot, xh, xl)
            out_phase(1, OUT1)


def kernel(**inputs):
    import concourse.bacc as bacc
    from concourse.bass_utils import run_bass_kernel_spmd

    def tiles(a):
        return np.asarray(a).reshape(-1, P).T

    arrays = {
        "x_t": np.ascontiguousarray(np.asarray(inputs["x"])[0].T),
        "params": np.ascontiguousarray(np.concatenate(
            [tiles(inputs["norm_g"]), tiles(inputs["sc_conv_w"]), tiles(inputs["sc_conv_b"])], axis=1)),
    }
    for name in ("sb_w_in", "sb_w_out", "sc_w_in", "sc_w_out"):
        arrays[name] = np.ascontiguousarray(inputs[name])
    nc = bacc.Bacc("TRN2", target_bir_lowering=False, num_devices=1)
    args = [nc.dram_tensor(name, a.shape, mybir.dt.from_np(a.dtype), kind="ExternalInput").ap() for name, a in arrays.items()]
    args.append(nc.dram_tensor("x1_t", (D, SEQ), F32, kind="Internal").ap())
    args.append(nc.dram_tensor("out_t", (D, SEQ), F32, kind="ExternalOutput").ap())
    trunk(nc, *args)
    r = run_bass_kernel_spmd(nc, [arrays], core_ids=[0])
    return np.ascontiguousarray(r.results[0]["out_t"].T)[None]
```
